# Optimizing a Trainium2 kernel written in Bass

```python
import jax, jax.numpy as jnp
from jax import lax
import numpy as np

D_MODEL = 1024
BATCH = 1
SEQ = 256
DEPTH = 4

N_MIXERS = 3
SB_HEADS = 16
SB_HEAD_DIM = D_MODEL // SB_HEADS
SB_BLOCK = 128
SSD_EXPAND = 2
SSD_D_INNER = SSD_EXPAND * D_MODEL
SSD_HEAD_DIM = 64
SSD_HEADS = SSD_D_INNER // SSD_HEAD_DIM
SSD_GROUPS = 8
SSD_HPG = SSD_HEADS // SSD_GROUPS
SSD_STATE = 128
SSD_CONV = 4
SSD_CHUNK = 128
SSD_CONV_DIM = SSD_D_INNER + 2 * SSD_GROUPS * SSD_STATE
SSD_IN_DIM = SSD_D_INNER + SSD_CONV_DIM + SSD_HEADS
SSD_NORM_GROUP = SSD_D_INNER // SSD_GROUPS
SC_WIDTH = 3
D_FF = 2816
RMS_EPS = 1e-6
N_SB_LAYERS = (DEPTH + 2) // 3
N_SSD_LAYERS = (DEPTH + 1) // 3
N_SC_LAYERS = DEPTH // 3

kernel_name = "hybrid_sb_ssd_shortconv_macaron"

def rmsnorm(x, g):
    xf = x.astype(jnp.float32)
    y = xf * lax.rsqrt(jnp.mean(xf * xf, axis=-1, keepdims=True) + RMS_EPS)
    return (y * g.astype(jnp.float32)).astype(x.dtype)

def swiglu(x, w_gu, w_down):
    gate, up = jnp.split(x @ w_gu, 2, axis=-1)
    return (jax.nn.silu(gate) * up) @ w_down

def causal_depthwise_conv(x, w):
    k, c = w.shape
    return lax.conv_general_dilated(
        x, w[:, None, :].astype(x.dtype), window_strides=(1,), padding=[(k - 1, 0)],
        dimension_numbers=('NWC', 'WIO', 'NWC'), feature_group_count=c)

def stick_breaking_attention(x, w_qkv, w_o):
    b, l, _ = x.shape
    q, k, v = jnp.split(x @ w_qkv, 3, axis=-1)
    q = q.reshape(b, l, SB_HEADS, SB_HEAD_DIM)
    k = k.reshape(b, l, SB_HEADS, SB_HEAD_DIM)
    v = v.reshape(b, l, SB_HEADS, SB_HEAD_DIM)
    n_blk = l // SB_BLOCK
    q_blocks = jnp.moveaxis(q.reshape(b, n_blk, SB_BLOCK, SB_HEADS, SB_HEAD_DIM), 1, 0)
    key_pos = jnp.arange(l)
    scale = SB_HEAD_DIM ** -0.5

    def one_block(args):
        q_blk, blk = args
        z = jnp.einsum('bqhd,bkhd->bhqk', q_blk, k).astype(jnp.float32) * scale
        q_pos = blk * SB_BLOCK + jnp.arange(SB_BLOCK)
        mask = key_pos[None, :] < q_pos[:, None]
        log_beta = jax.nn.log_sigmoid(z)
        log_keep = jnp.where(mask, jax.nn.log_sigmoid(-z), 0.0)
        tail = lax.cumsum(log_keep, axis=3, reverse=True) - log_keep
        att = jnp.where(mask, jnp.exp(log_beta + tail), 0.0)
        return jnp.einsum('bhqk,bkhd->bqhd', att.astype(v.dtype), v)

    o = lax.map(one_block, (q_blocks, jnp.arange(n_blk)))
    o = jnp.moveaxis(o, 0, 1).reshape(b, l, D_MODEL)
    return o @ w_o

def ssd_chunked(xs, dt, a, bm, cm):
    b, l, g, r, p = xs.shape
    n = bm.shape[-1]
    nc, cl = l // SSD_CHUNK, SSD_CHUNK
    x_c = xs.reshape(b, nc, cl, g, r, p)
    dt_c = dt.reshape(b, nc, cl, g, r)
    b_c = bm.reshape(b, nc, cl, g, n)
    c_c = cm.reshape(b, nc, cl, g, n)
    a_cum = jnp.cumsum(dt_c * a, axis=2)
    seg = a_cum[:, :, :, None] - a_cum[:, :, None, :]
    causal = jnp.tril(jnp.ones((cl, cl), dtype=bool))[:, :, None, None]
    decay = jnp.exp(jnp.where(causal, seg, -jnp.inf))
    cb = jnp.einsum('bclgn,bcsgn->bclsg', c_c, b_c)
    w = cb[..., None] * decay * dt_c[:, :, None]
    y_diag = jnp.einsum('bclsgr,bcsgrp->bclgrp', w, x_c)
    a_last = a_cum[:, :, -1]
    to_end = jnp.exp(a_last[:, :, None] - a_cum) * dt_c
    states = jnp.einsum('bcsgn,bcsgr,bcsgrp->bcgrpn', b_c, to_end, x_c)

    def step(h, inp):
        st, al = inp
        return h * jnp.exp(al)[..., None, None] + st, h

    h0 = jnp.zeros((b, g, r, p, n), dtype=xs.dtype)
    _, h_prev = lax.scan(step, h0, (jnp.moveaxis(states, 1, 0), jnp.moveaxis(a_last, 1, 0)))
    h_prev = jnp.moveaxis(h_prev, 0, 1)
    y_off = jnp.einsum('bclgn,bcgrpn,bclgr->bclgrp', c_c, h_prev, jnp.exp(a_cum))
    return (y_diag + y_off).reshape(b, l, g, r, p)

def ssd_mixer(x, w_in, conv_w, conv_b, dt_bias, a_log, d_skip, norm_g, w_out):
    b, l, _ = x.shape
    z, xbc, dt = jnp.split(x @ w_in, [SSD_D_INNER, SSD_D_INNER + SSD_CONV_DIM], axis=-1)
    xbc = jax.nn.silu(causal_depthwise_conv(xbc, conv_w) + conv_b)
    xs, bm, cm = jnp.split(xbc, [SSD_D_INNER, SSD_D_INNER + SSD_GROUPS * SSD_STATE], axis=-1)
    xs = xs.astype(jnp.float32).reshape(b, l, SSD_GROUPS, SSD_HPG, SSD_HEAD_DIM)
    bm = bm.astype(jnp.float32).reshape(b, l, SSD_GROUPS, SSD_STATE)
    cm = cm.astype(jnp.float32).reshape(b, l, SSD_GROUPS, SSD_STATE)
    dt = jax.nn.softplus(dt.astype(jnp.float32) + dt_bias.astype(jnp.float32))
    dt = dt.reshape(b, l, SSD_GROUPS, SSD_HPG)
    a = -jnp.exp(a_log.astype(jnp.float32)).reshape(SSD_GROUPS, SSD_HPG)
    y = ssd_chunked(xs, dt, a, bm, cm)
    y = y + d_skip.astype(jnp.float32).reshape(SSD_GROUPS, SSD_HPG, 1) * xs
    y = y.reshape(b, l, SSD_D_INNER).astype(x.dtype) * jax.nn.silu(z)
    y = rmsnorm(y.reshape(b, l, SSD_GROUPS, SSD_NORM_GROUP),
                norm_g.reshape(SSD_GROUPS, SSD_NORM_GROUP)).reshape(b, l, SSD_D_INNER)
    return y @ w_out

def short_conv_mixer(x, w_in, conv_w, w_out):
    b_gate, c_gate, h = jnp.split(x @ w_in, 3, axis=-1)
    u = causal_depthwise_conv(c_gate * h, conv_w)
    return (b_gate * u) @ w_out

def setup_inputs(seed: int = 0) -> dict:
    key = jax.random.key(seed)
    ks = jax.random.split(key, 24)
    f32 = jnp.float32

    def wn(k, shape, fan_in):
        return jax.random.normal(k, shape, f32) * (fan_in ** -0.5)

    def gain(k, shape):
        return 1.0 + 0.01 * jax.random.normal(k, shape, f32)

    dt0 = jnp.exp(jax.random.uniform(ks[14], (N_SSD_LAYERS, SSD_HEADS), f32)
                  * (np.log(0.1) - np.log(0.001)) + np.log(0.001))
    dt_bias = dt0 + jnp.log(-jnp.expm1(-dt0))
    return {
        "x": jax.random.normal(ks[0], (BATCH, SEQ, D_MODEL), f32),
        "ffn1_norm": gain(ks[1], (DEPTH, D_MODEL)),
        "ffn1_w_gu": wn(ks[2], (DEPTH, D_MODEL, 2 * D_FF), D_MODEL),
        "ffn1_w_down": wn(ks[3], (DEPTH, D_FF, D_MODEL), D_FF),
        "mix_norm": gain(ks[4], (DEPTH, D_MODEL)),
        "ffn2_norm": gain(ks[5], (DEPTH, D_MODEL)),
        "ffn2_w_gu": wn(ks[6], (DEPTH, D_MODEL, 2 * D_FF), D_MODEL),
        "ffn2_w_down": wn(ks[7], (DEPTH, D_FF, D_MODEL), D_FF),
        "sb_w_qkv": wn(ks[8], (N_SB_LAYERS, D_MODEL, 3 * D_MODEL), D_MODEL),
        "sb_w_o": wn(ks[9], (N_SB_LAYERS, D_MODEL, D_MODEL), D_MODEL),
        "ssd_w_in": wn(ks[10], (N_SSD_LAYERS, D_MODEL, SSD_IN_DIM), D_MODEL),
        "ssd_conv_w": wn(ks[11], (N_SSD_LAYERS, SSD_CONV, SSD_CONV_DIM), SSD_CONV),
        "ssd_conv_b": 0.01 * jax.random.normal(ks[12], (N_SSD_LAYERS, SSD_CONV_DIM), f32),
        "ssd_dt_bias": dt_bias,
        "ssd_a_log": jnp.log(jax.random.uniform(ks[15], (N_SSD_LAYERS, SSD_HEADS), f32, 1.0, 16.0)),
        "ssd_d": gain(ks[16], (N_SSD_LAYERS, SSD_HEADS)),
        "ssd_norm": gain(ks[17], (N_SSD_LAYERS, SSD_D_INNER)),
        "ssd_w_out": wn(ks[18], (N_SSD_LAYERS, SSD_D_INNER, D_MODEL), SSD_D_INNER),
        "sc_w_in": wn(ks[19], (N_SC_LAYERS, D_MODEL, 3 * D_MODEL), D_MODEL),
        "sc_conv_w": wn(ks[20], (N_SC_LAYERS, SC_WIDTH, D_MODEL), SC_WIDTH),
        "sc_w_out": wn(ks[21], (N_SC_LAYERS, D_MODEL, D_MODEL), D_MODEL),
        "final_norm": gain(ks[22], (D_MODEL,)),
    }

def reference(x, ffn1_norm, ffn1_w_gu, ffn1_w_down, mix_norm, ffn2_norm, ffn2_w_gu, ffn2_w_down,
              sb_w_qkv, sb_w_o, ssd_w_in, ssd_conv_w, ssd_conv_b, ssd_dt_bias, ssd_a_log, ssd_d,
              ssd_norm, ssd_w_out, sc_w_in, sc_conv_w, sc_w_out, final_norm):
    for i in range(DEPTH):
        x = x + 0.5 * swiglu(rmsnorm(x, ffn1_norm[i]), ffn1_w_gu[i], ffn1_w_down[i])
        h = rmsnorm(x, mix_norm[i])
        kind, j = i % N_MIXERS, i // N_MIXERS
        if kind == 0:
            m = stick_breaking_attention(h, sb_w_qkv[j], sb_w_o[j])
        elif kind == 1:
            m = ssd_mixer(h, ssd_w_in[j], ssd_conv_w[j], ssd_conv_b[j], ssd_dt_bias[j],
                          ssd_a_log[j], ssd_d[j], ssd_norm[j], ssd_w_out[j])
        else:
            m = short_conv_mixer(h, sc_w_in[j], sc_conv_w[j], sc_w_out[j])
        x = x + m
        x = x + 0.5 * swiglu(rmsnorm(x, ffn2_norm[i]), ffn2_w_gu[i], ffn2_w_down[i])
    return rmsnorm(x, final_norm)


_drawn_inputs = setup_inputs


def setup_inputs(seed=0):
    import zlib

    import numpy as np

    out = dict(_drawn_inputs(seed))
    spreads = {}
    factors = {'ffn1_norm': 5.483,
     'mix_norm': 2.973,
     'ffn2_norm': 7.427,
     'ssd_conv_b': 26.811,
     'ssd_d': 64.0,
     'ssd_norm': 56.256,
     'final_norm': 31.819}
    for name, (base, spread) in spreads.items():
        noise = np.random.default_rng([zlib.crc32(name.encode()), seed]).standard_normal(out[name].shape)
        drawn = base * np.exp(spread * noise) if base else spread * noise
        out[name] = __import__('jax').numpy.asarray(drawn.astype(out[name].dtype))
    for name, factor in factors.items():
        out[name] = (out[name] * factor).astype(out[name].dtype)
    return out
```

```python
from contextlib import ExitStack

import concourse.bass as bass
from concourse import mybir

F32 = mybir.dt.float32
F32R = mybir.dt.float32r
ACT = mybir.ActivationFunctionType
ALU = mybir.AluOpType
P = 128

SEQ, D, DFF = 256, 1024, 2816
HALVES = SEQ // P
KD = D // P
NB = D // 512
QUARTERS = NB * HALVES
FFN_W = 256
GROUPS = DFF // FFN_W
EPS = 1e-6
HEADS, HEAD_DIM = 16, 64
HEADS_PER_J = 4
SSD_IN, SSD_INNER, SSD_G, SSD_HPG, SSD_P, SSD_N = 6176, 2048, 8, 4, 64, 128
SSD_HEADS = SSD_G * SSD_HPG
SSD_CONV, SSD_CONV_DIM = 4, 4096
SC_W = 3
ARENA = 16000
LOG_EXP_SET = 6

BLOCK = 2048
SPLIT_SLOTS = 3
STAGE_SLOTS = 3

PHASES = [("ffn", 0, 0), ("attention", 0, 0), ("ffn", 0, 1),
          ("ffn", 1, 0), ("ssd", 1, 0), ("ffn", 1, 1),
          ("ffn", 2, 0), ("conv", 2, 0), ("ffn", 2, 1),
          ("ffn", 3, 0), ("attention", 3, 1), ("ffn", 3, 1)]
BLOCKS = {"ffn": 3 * GROUPS, "attention": 4 + 8 + 4, "ssd": 1 + 8 + 16 + 8, "conv": 16 + 4}


def at(value, step=None, per_step=0):
    return value if step is None else step * per_step + value


def build_trunk(nc, x, ffn1_norm, ffn1_w_gu, ffn1_w_down, mix_norm, ffn2_norm, ffn2_w_gu,
                ffn2_w_down, sb_w_qkv, sb_w_o, ssd_w_in, ssd_conv_w, ssd_conv_b, ssd_dt_bias,
                ssd_a_log, ssd_d, ssd_norm, ssd_w_out, sc_w_in, sc_conv_w, sc_w_out, final_norm,
                out):
    base, total = [], 0
    for kind, _, _ in PHASES:
        base.append(total)
        total += BLOCKS[kind]
    base.append(total)
    n_phases = len(PHASES)

    def nth(kind, p):
        return sum(1 for k, _, _ in PHASES[:p] if k == kind)

    def before(p, **per_phase):
        return sum(per_phase.get(k, 0) for k, _, _ in PHASES[:p])

    def mixers_before(p):
        return before(p, attention=1, ssd=1, conv=1)

    def raw_base(p):
        return before(p, ssd=3 * SSD_G, conv=2 * KD)

    def chan_base(p):
        return before(p, ssd=4 * SSD_G, conv=KD)

    def tap_base(p):
        return before(p, ssd=3 * 4 * SSD_G, conv=SC_W * KD)

    def src_base(p):
        return before(p, ssd=SSD_G, conv=KD)

    def mt_base(p):
        return before(p, attention=4, ssd=SSD_G, conv=KD)

    def mtp_base(p):
        return before(p, attention=4, ssd=SSD_G)

    def ssd_chunk(g, c):
        return (2 * g, 2 * g + 1, SSD_INNER // P + g, SSD_INNER // P + SSD_G + g)[c]

    def out_blocks(kind):
        return {"attention": (12, 2), "ssd": (25, 4), "conv": (16, 2)}[kind]

    def rows(w, r0, nr, c0, nc_):
        return w[r0:r0 + nr * P, c0:c0 + nc_].rearrange("(k p) c -> p k c", p=P)

    def mixer_block(kind, index, i):
        if kind == "attention":
            wqkv, wo = sb_w_qkv[index], sb_w_o[index]
            if i < 4:
                n, kh = divmod(i, 2)
                return [(0, 512, 4, 512, rows(wqkv, 512 * kh, 4, 2 * D + 512 * n, 512))]
            if i < 12:
                j, kh = divmod(i - 4, 2)
                return [(0, 256, 4, 512, rows(wqkv, 512 * kh, 4, 256 * j, 256)),
                        (256, 256, 4, 512, rows(wqkv, 512 * kh, 4, D + 256 * j, 256))]
            n, kh = divmod(i - 12, 2)
            return [(0, 512, 4, 512, rows(wo, 512 * kh, 4, 512 * n, 512))]
        if kind == "ssd":
            win, wout = ssd_w_in[index], ssd_w_out[index]
            if i == 0:
                return [(0, SSD_HEADS, KD, SSD_HEADS, rows(win, 0, KD, SSD_IN - SSD_HEADS, SSD_HEADS))]
            if i < 9:
                n, kh = divmod(i - 1, 2)
                return [(0, 512, 4, 512, rows(win, 512 * kh, 4, 512 * n, 512))]
            if i < 25:
                g, kh = divmod(i - 9, 2)
                b0 = 2 * SSD_INNER
                return [(0, 256, 4, 512, rows(win, 512 * kh, 4, SSD_INNER + 256 * g, 256)),
                        (256, 128, 4, 512, rows(win, 512 * kh, 4, b0 + P * g, P)),
                        (384, 128, 4, 512, rows(win, 512 * kh, 4, b0 + SSD_G * SSD_N + P * g, P))]
            n, kq = divmod(i - 25, 4)
            return [(0, 512, 4, 512, rows(wout, 512 * kq, 4, 512 * n, 512))]
        win, wout = sc_w_in[index], sc_w_out[index]
        if i < 16:
            j, kh = divmod(i, 2)
            return [(P * s, P, 4, 3 * P, rows(win, 512 * kh, 4, D * c + P * j, P))
                    for s, c in enumerate((1, 2, 0))]
        n, kh = divmod(i - 16, 2)
        return [(0, 512, 4, 512, rows(wout, 512 * kh, 4, 512 * n, 512))]

    def block_columns(n):
        p = max(q for q in range(n_phases) if base[q] <= n)
        kind, i = PHASES[p][0], n - base[p]
        if kind == "ssd" and i == 0:
            return KD * SSD_HEADS
        return 4 * 3 * P if kind == "conv" and i < 16 else BLOCK

    loaded, so_far = [], [0] * STAGE_SLOTS
    for p, (kind, _, index) in enumerate(PHASES):
        for i in range(BLOCKS[kind]):
            n = base[p] + i
            so_far[n % STAGE_SLOTS] += 16 * (2 if kind == "ffn" else len(mixer_block(kind, index, i)))
            loaded.append(so_far[n % STAGE_SLOTS])

    def blk_a(p, g):
        return base[p] + (0 if g == 0 else 3 * g - 1)

    def blk_b(p, g):
        return base[p] + (1 if g == 0 else 3 * g)

    def blk_d(p, g):
        return base[p] + (3 * g + 4 if g < GROUPS - 1 else 3 * g + 2)

    LOOP_FROM, LOOP_TO = 2, GROUPS - 1
    LOOP_BLOCKS = 6

    ctx = ExitStack()
    with ctx:
        ctx.enter_context(nc.allow_non_contiguous_dma(reason="parameter rows"))

        def sb(name, shape, dt=F32):
            return ctx.enter_context(nc.sbuf_tensor(name, shape, dt))

        def sem(name):
            return ctx.enter_context(nc.semaphore(name))

        stage = [sb(f"stage{i}", [P, BLOCK]) for i in range(STAGE_SLOTS)]
        w_hi = [sb(f"w_hi{i}", [P, BLOCK], F32R) for i in range(SPLIT_SLOTS)]
        w_lo = [sb(f"w_lo{i}", [P, BLOCK], F32R) for i in range(SPLIT_SLOTS)]
        x_res = sb("x_res", [P, HALVES, D])
        xt_hi = sb("xt_hi", [P, KD, SEQ], F32R)
        xt_lo = sb("xt_lo", [P, KD, SEQ], F32R)
        ht_hi = sb("ht_hi", [P, 2, SEQ], F32R)
        ht_lo = sb("ht_lo", [P, 2, SEQ], F32R)
        mt_hi = sb("mt_hi", [P, 2 * KD, SEQ], F32R)
        mt_lo = sb("mt_lo", [P, 2 * KD, SEQ], F32R)
        N_NORM, N_TAP = 3 * 4 * KD, SSD_CONV * SSD_CONV_DIM // P
        N_REST = SSD_INNER // P + SSD_CONV_DIM // P + SC_W * KD
        par = sb("par", [P, N_NORM + N_TAP + N_REST])
        ident = sb("ident", [P, P])
        ones = sb("ones", [P, P])
        upper = sb("upper", [P, P])
        neg_lower = sb("neg_lower", [P, P])
        neg_ones = sb("neg_ones", [P, P])
        keep = sb("keep", [P, P])
        bar = sb("bar", [P, P])
        ss = sb("ss", [P, QUARTERS])
        ms = sb("ms", [P, 4])
        rstd = sb("rstd", [P, 2])
        neg_half = sb("neg_half", [P, 2])
        arena = sb("arena", [P, ARENA])
        used = [0]

        def area(n, fresh=False):
            if fresh:
                used[0] = 0
            v = arena[:, used[0]:used[0] + n]
            used[0] += n
            assert used[0] <= ARENA, used[0]
            return v

        xg = area(QUARTERS * 512, True).rearrange("p (i c) -> p i c", i=QUARTERS)
        xn = area(HALVES * D).rearrange("p (h c) -> p h c", h=HALVES)
        squares = area(QUARTERS * 512).rearrange("p (i c) -> p i c", i=QUARTERS)
        sg = area(2 * FFN_W).rearrange("p (h c) -> p h c", h=2)
        hid = area(2 * FFN_W).rearrange("p (h c) -> p h c", h=2)
        par_rows = area(3 * P).rearrange("p (t c) -> p t c", t=3)
        final_gain = area(D)
        v_sb = area(HALVES * D, True).rearrange("p (h c) -> p h c", h=HALVES)
        q_t = area(2 * 2 * SEQ).rearrange("p (b c t) -> p b c t", b=2, c=2)
        k_t = area(2 * 2 * SEQ).rearrange("p (b c t) -> p b c t", b=2, c=2)
        z_abs = area(2 * 384).rearrange("p (b c) -> p b c", b=2)
        z_exp = area(2 * 384).rearrange("p (b c) -> p b c", b=2)
        z_ln = area(2 * 384).rearrange("p (b c) -> p b c", b=2)
        softplus = area(2 * 384).rearrange("p (b c) -> p b c", b=2)
        log_att = area(2 * 384).rearrange("p (b c) -> p b c", b=2)
        att = area(2 * 384).rearrange("p (b c) -> p b c", b=2)
        o_sb = area(2 * 256).rearrange("p (h c) -> p h c", h=2)
        CH = 2 * SSD_HEADS
        decay = area(SSD_G * 2 * SSD_HPG * P, True).rearrange(
            "p (g c r l) -> p g c r l", g=SSD_G, c=2, r=SSD_HPG)
        z_sb = area(HALVES * SSD_INNER).rearrange("p (h c) -> p h c", h=HALVES)
        chan = area(4 * SEQ).rearrange("p (c t) -> p c t", c=4)
        xdt = area(2 * 256).rearrange("p (h c) -> p h c", h=2)
        xd = area(2 * 256).rearrange("p (h c) -> p h c", h=2)
        x_end = area(256)
        h_prev = x_end
        b_tok = area(P)
        cb = area(2 * P).rearrange("p (c l) -> p c l", c=2)
        y_sb = area(2 * 256).rearrange("p (h c) -> p h c", h=2)
        yg = area(2 * 256).rearrange("p (h c) -> p h c", h=2)
        c_sb = area(2 * SEQ, True).rearrange("p (b t) -> p b t", b=2)
        ch = area(2 * SEQ).rearrange("p (b t) -> p b t", b=2)
        u_sb = area(2 * SEQ).rearrange("p (b t) -> p b t", b=2)
        bu = area(2 * SEQ).rearrange("p (b t) -> p b t", b=2)

        dt_bias_bc = sb("dt_bias_bc", [P, SSD_HEADS])
        a_log_bc = sb("a_log_bc", [P, SSD_HEADS])
        d_bc = sb("d_bc", [P, SSD_HEADS])
        dts = sb("dts", [P, 9, CH])
        acum = sb("acum", [P, CH])
        e_off = sb("e_off", [P, SSD_HEADS])
        to_end = sb("to_end", [P, SSD_HEADS])
        yss = sb("yss", [P, 2])
        yms = sb("yms", [P, 4])
        yrstd = sb("yrstd", [P, 2])

        bank = [ctx.enter_context(nc.psum_tensor(f"bank{i}", [P, 512], F32)) for i in range(8)]
        up = bank[4:6]
        tb = bank[6:8]

        def acc(i):
            return bank[i]

        stage_in = [sem(f"stage_in{i}") for i in range(STAGE_SLOTS)]
        hi_done = sem("hi_done")
        lo_done = sem("lo_done")
        block_used = sem("block_used")
        x_in = sem("x_in")
        par_in = sem("par_in")
        bc_in = sem("bc_in")
        gain_in = sem("gain_in")
        out_done = sem("out_done")
        const_zero = sem("const_zero")
        const_done = sem("const_done")
        par_ps = sem("par_ps")
        par_sb = sem("par_sb")
        acc_ready = sem("acc_ready")
        x_updated = sem("x_updated")
        sq_done = sem("sq_done")
        rms_step = sem("rms_step")
        rstd_done = sem("rstd_done")
        xn_done = sem("xn_done")
        xt_ps = sem("xt_ps")
        xg_done = sem("xg_done")
        xt_hi_done = sem("xt_hi_done")
        xt_lo_done = sem("xt_lo_done")
        half0_done = sem("half0_done")
        silu_done = sem("silu_done")
        gated = sem("gated")
        ht_ps = sem("ht_ps")
        ht_hi_done = sem("ht_hi_done")
        ht_lo_done = sem("ht_lo_done")
        mt_ps = sem("mt_ps")
        mt_src = sem("mt_src")
        mt_hi_done = sem("mt_hi_done")
        mt_lo_done = sem("mt_lo_done")
        v_ps, v_done = sem("v_ps"), sem("v_done")
        qk_ps, qk_done = sem("qk_ps"), sem("qk_done")
        z_ps, abs_done, exp_done, ln_done = sem("z_ps"), sem("abs_done"), sem("exp_done"), sem("ln_done")
        sp_step, sp_done = sem("sp_step"), sem("sp_done")
        cum_ps, log_att_done, att_done = sem("cum_ps"), sem("log_att_done"), sem("att_done")
        o_ps, o_done = sem("o_ps"), sem("o_done")
        dt_act, dt_dve = sem("dt_act"), sem("dt_dve")
        cum2_ps, seg_ps, seg_done, decay_done = sem("cum2_ps"), sem("seg_ps"), sem("seg_done"), sem("decay_done")
        zz_ps, zz_done = sem("zz_ps"), sem("zz_done")
        raw_ps, tap_first, tap_done, chan_done = sem("raw_ps"), sem("tap_first"), sem("tap_done"), sem("chan_done")
        tok_ps, tok_act, tok_dve = sem("tok_ps"), sem("tok_act"), sem("tok_dve")
        xdt_done = sem("xdt_done")
        wdec_done, hp_ps, hp_done, y_ps = sem("wdec_done"), sem("hp_ps"), sem("hp_done"), sem("y_ps")
        y_step, y_act, y_pool, y_rstd, y_done = sem("y_step"), sem("y_act"), sem("y_pool"), sem("y_rstd"), sem("y_done")

        block = ctx.enter_context(nc.Block())

        gain_of = {("ffn", 0): 0, ("ffn", 1): 2 * 4 * KD}

        def acc_wait(eng, p, i):
            kind = PHASES[p][0]
            if i == 3:
                eng.wait_ge(block_used, base[p + 1])
            elif kind == "ffn":
                eng.wait_ge(acc_ready, before(p, ffn=3, attention=2, ssd=2, conv=2) + i + 1)
            elif i == 1:
                first, nk = out_blocks(kind)
                eng.wait_ge(block_used, base[p] + first + nk)
            else:
                eng.wait_ge(acc_ready, before(p, ffn=3, attention=2, ssd=2, conv=2) + i // 2 + 1)

        def gains(p):
            kind, layer, which = PHASES[p]
            first = 4 * KD if kind != "ffn" else gain_of[("ffn", which)]
            return first + KD * layer

        TAPS = N_NORM
        YNORM = N_NORM + N_TAP
        CBIAS = YNORM + SSD_INNER // P
        SCTAPS = CBIAS + SSD_CONV_DIM // P

        @block.sync
        def _(sp):
            for h in range(HALVES):
                sp.dma_start(x_res[:, h, :], x[0, h * P:(h + 1) * P, :]).then_inc(x_in, 16)
            n_par = 0
            for t, r0, src in ((0, 0, ffn1_norm), (0, 32, mix_norm), (0, 64, ffn2_norm)):
                sp.dma_start(par_rows[r0:r0 + 32, t, :], src.rearrange("l (k c) -> (l k) c", c=P)).then_inc(par_in, 16)
            sp.dma_start(par_rows[0:N_TAP, 1, :], ssd_conv_w[0].rearrange("w (k c) -> (w k) c", c=P)).then_inc(par_in, 16)
            sp.dma_start(par_rows[0:16, 2, :], ssd_norm.rearrange("l (k c) -> (l k) c", c=P)).then_inc(par_in, 16)
            sp.dma_start(par_rows[16:48, 2, :], ssd_conv_b.rearrange("l (k c) -> (l k) c", c=P)).then_inc(par_in, 16)
            sp.dma_start(par_rows[48:72, 2, :], sc_conv_w[0].rearrange("w (k c) -> (w k) c", c=P)).then_inc(par_in, 16)

            def free_slot(n, step=None):
                if n >= STAGE_SLOTS:
                    sp.wait_ge(lo_done, at(n - STAGE_SLOTS + 1, step, LOOP_BLOCKS))

            def ffn_cols(g, step):
                return FFN_W * g if step is None else step * (2 * FFN_W) + FFN_W * g

            def load_gate_up(p, g, kh, n, step=None):
                free_slot(n, step)
                _, layer, which = PHASES[p]
                w = (ffn1_w_gu, ffn2_w_gu)[which][layer, 512 * kh:512 * (kh + 1), :].rearrange("(k p) c -> p k c", p=P)
                dst = stage[n % STAGE_SLOTS][:, :].rearrange("p (k c) -> p k c", k=4)
                for part in range(2):
                    c0 = ffn_cols(g, step) + DFF * part
                    sp.dma_start(dst[:, :, FFN_W * part:FFN_W * (part + 1)],
                                 w[:, :, bass.ds(c0, FFN_W)]).then_inc(stage_in[n % STAGE_SLOTS], 16)

            def load_down(p, g, n, step=None):
                free_slot(n, step)
                _, layer, which = PHASES[p]
                w = (ffn1_w_down, ffn2_w_down)[which][layer]
                for j in range(2):
                    r0 = ffn_cols(g, step) + P * j
                    sp.dma_start(stage[n % STAGE_SLOTS][:, D * j:D * (j + 1)],
                                 w[bass.ds(r0, P), :]).then_inc(stage_in[n % STAGE_SLOTS], 16)

            def load_group(p, g, step=None):
                load_gate_up(p, g, 0, blk_a(p, g), step)
                load_gate_up(p, g, 1, blk_b(p, g), step)
                if g >= 1:
                    load_down(p, g - 1, blk_d(p, g - 1), step)

            for p, (kind, layer, index) in enumerate(PHASES):
                if kind == "ffn":
                    for g in range(LOOP_FROM):
                        load_group(p, g)
                    with sp.Fori(0, (LOOP_TO - LOOP_FROM) // 2) as step:
                        for g in (LOOP_FROM, LOOP_FROM + 1):
                            load_group(p, g, step)
                    load_group(p, GROUPS - 1)
                    load_down(p, GROUPS - 1, blk_d(p, GROUPS - 1))
                else:
                    for i in range(BLOCKS[kind]):
                        n = base[p] + i
                        free_slot(n)
                        for c0, cols, k, width, src in mixer_block(kind, index, i):
                            dst = stage[n % STAGE_SLOTS][:, 0:k * width].rearrange("p (k c) -> p k c", k=k)
                            sp.dma_start(dst[:, :, c0:c0 + cols], src).then_inc(stage_in[n % STAGE_SLOTS], 16)
            sp.dma_start(final_gain, final_norm.rearrange("(a d) -> a d", a=1).to_broadcast([P, D])).then_inc(gain_in, 16)
            for h in range(HALVES):
                sp.wait_ge(xn_done, 2 * mixers_before(n_phases) + h + 1)
                sp.dma_start(out[0, h * P:(h + 1) * P, :], xn[:, h, :]).then_inc(out_done, 16)
            sp.wait_ge(out_done, 16 * HALVES)

        @block.gpsimd
        def _(pool):
            pool.dma_start(dt_bias_bc[:, :], ssd_dt_bias.to_broadcast([P, SSD_HEADS])).then_inc(bc_in, 16)
            pool.dma_start(a_log_bc[:, :], ssd_a_log.to_broadcast([P, SSD_HEADS])).then_inc(bc_in, 16)
            pool.dma_start(d_bc[:, :], ssd_d.to_broadcast([P, SSD_HEADS])).then_inc(bc_in, 16)
            pool.memset(neg_half[:, :], -0.5).then_inc(const_zero, 1)
            pool.memset(ident[:, :], 0.0).then_inc(const_zero, 1)
            pool.memset(ones[:, :], 1.0).then_inc(const_zero, 1)
            pool.memset(upper[:, :], 1.0).then_inc(const_zero, 1)
            pool.memset(neg_lower[:, :], -1.0).then_inc(const_zero, 1)
            pool.memset(neg_ones[:, :], -1.0).then_inc(const_zero, 1)
            pool.memset(keep[:, :], 1.0).then_inc(const_zero, 1)
            pool.memset(bar[:, :], 0.0).then_inc(const_zero, 1)
            pool.wait_ge(const_zero, 8)
            pool.affine_select(out=ident[:, :], in_=ident[:, :], compare_op=ALU.not_equal, fill=1.0,
                               base=0, pattern=[[-1, P]], channel_multiplier=1).then_inc(const_done, 1)
            pool.affine_select(out=upper[:, :], in_=upper[:, :], compare_op=ALU.is_ge, fill=0.0,
                               base=0, pattern=[[1, P]], channel_multiplier=-1).then_inc(const_done, 1)
            pool.affine_select(out=neg_lower[:, :], in_=neg_lower[:, :], compare_op=ALU.is_ge, fill=0.0,
                               base=0, pattern=[[-1, P]], channel_multiplier=1).then_inc(const_done, 1)
            pool.affine_select(out=keep[:, :], in_=keep[:, :], compare_op=ALU.is_gt, fill=0.0,
                               base=0, pattern=[[1, P]], channel_multiplier=-1).then_inc(const_done, 1)
            pool.affine_select(out=bar[:, :], in_=bar[:, :], compare_op=ALU.is_gt, fill=-1e30,
                               base=0, pattern=[[1, P]], channel_multiplier=-1).then_inc(const_done, 1)

            def root(mean, t, result, step_sem, first, done, scale):
                pool.tensor_scalar(t[:, 2:4], mean, scale, EPS, ALU.mult, ALU.add).then_inc(step_sem, 1)
                pool.wait_ge(step_sem, first)
                pool.tensor_tensor(result, t[:, 2:4], neg_half[:, :], ALU.pow).then_inc(done, 1)

            def phase_rstd(p):
                pool.wait_ge(sq_done, QUARTERS * (p + 1))
                pool.tensor_tensor(ms[:, 0:2], ss[:, 0:2], ss[:, 2:4], ALU.add).then_inc(rms_step, 1)
                pool.wait_ge(rms_step, 2 * p + 1)
                root(ms[:, 0:2], ms, rstd[:, :], rms_step, 2 * p + 2, rstd_done, 1.0 / D)

            for p in range(n_phases + 1):
                phase_rstd(p)
                if p < n_phases and PHASES[p][0] == "ssd":
                    for g in range(SSD_G):
                        pool.wait_ge(tok_dve, 4 * g + 2)
                        pool.wait_ge(decay_done, 2 * g + 2)
                        for c in range(2):
                            d = decay[:, g, c, :, :]
                            pool.tensor_tensor(d, d, cb[:, c:c + 1, :].to_broadcast([P, SSD_HPG, P]),
                                               ALU.mult).then_inc(wdec_done, 1)
                        pool.wait_ge(y_act, 3 * (g + 1))
                        root(yss[:, :], yms, yrstd[:, :], y_pool, g + 1, y_rstd, 1.0 / (SSD_INNER // SSD_G))

        @block.scalar
        def _(act):
            def split(n, step=None):
                if n >= total:
                    return
                s, q, c = n % STAGE_SLOTS, n % SPLIT_SLOTS, block_columns(n)
                act.wait_ge(stage_in[s], at(loaded[n], step, 2 * LOOP_BLOCKS // STAGE_SLOTS * 16))
                if n >= SPLIT_SLOTS:
                    act.wait_ge(block_used, at(n - SPLIT_SLOTS + 1, step, LOOP_BLOCKS))
                act.activation(w_hi[q][:, 0:c], stage[s][:, 0:c], ACT.Copy).then_inc(hi_done, 1)

            def entry(p):
                kind = PHASES[p][0] if p < n_phases else None

                def square(i):
                    h, n = i % 2, i // 2
                    if p == 0:
                        act.wait_ge(x_in, 16 * HALVES)
                    else:
                        act.wait_ge(x_updated, QUARTERS * (p - 1) + i + 1)
                    act.activation(squares[:, i, :], x_res[:, h, 512 * n:512 * (n + 1)], ACT.Square,
                                   accum_out=ss[:, i:i + 1]).then_inc(sq_done, 1)

                def x_hi(i):
                    h, n = i % 2, i // 2
                    act.wait_ge(xg_done, QUARTERS * p + i + 1)
                    act.activation(xt_hi[:, 4 * n:4 * (n + 1), h * P:(h + 1) * P],
                                   xg[:, i, :].rearrange("p (k t) -> p k t", k=4),
                                   ACT.Copy).then_inc(xt_hi_done, 1)

                if kind == "ffn":
                    for i in range(QUARTERS):
                        square(i)
                        x_hi(i)
                else:
                    for i in range(QUARTERS):
                        square(i)
                    if kind is not None:
                        for i in range(QUARTERS):
                            x_hi(i)

            def ffn(p):
                f = nth("ffn", p)

                def hidden_hi(g, step=None):
                    G = GROUPS * f + g
                    act.wait_ge(ht_ps, at(G + 1, step, 2))
                    act.activation(ht_hi[:, :, :], tb[0][:, :].rearrange("p (j t) -> p j t", j=2),
                                   ACT.Copy).then_inc(ht_hi_done, 1)

                def silu(g, step=None):
                    G = GROUPS * f + g
                    for h in range(HALVES):
                        if h == 0:
                            act.wait_ge(half0_done, at(G + 1, step, 2))
                        else:
                            act.wait_ge(block_used, at(blk_b(p, g) + 1, step, LOOP_BLOCKS))
                        act.activation(sg[:, h, :], up[h][:, 0:FFN_W], ACT.Silu,
                                       scale=rstd[:, h:h + 1]).then_inc(silu_done, 1)

                def group(g, step=None):
                    if g >= 1:
                        split(base[p] + 3 * g + 1, step)
                        hidden_hi(g - 1, step)
                    split(base[p] + 3 * g + 2, step)
                    if g == 0:
                        act.wait_ge(rstd_done, p + 1)
                    silu(g, step)
                    split(base[p] + 3 * g + 3, step)

                for g in range(LOOP_FROM):
                    group(g)
                with act.Fori(0, (LOOP_TO - LOOP_FROM) // 2) as step:
                    for g in (LOOP_FROM, LOOP_FROM + 1):
                        group(g, step)
                group(GROUPS - 1)
                hidden_hi(GROUPS - 1)
                split(base[p + 1] + 1)

            def attention(p):
                a = nth("attention", p)
                b0 = base[p]
                split(b0 + 2)
                split(b0 + 3)
                act.add_instruction(mybir.InstLoadActFuncSet(
                    act_func_set_id=LOG_EXP_SET, name=nc.get_next_instruction_name(),
                    engine=mybir.EngineType.Activation))
                for n in range(NB):
                    for h in range(HALVES):
                        if h == 0:
                            act.wait_ge(v_ps, NB * a + n + 1)
                        else:
                            act.wait_ge(block_used, b0 + 2 * n + 2)
                        act.activation(v_sb[:, h, 512 * n:512 * (n + 1)], bank[4 + 2 * n + h][:, :],
                                       ACT.Copy).then_inc(v_done, 1)
                    split(b0 + 4 + 2 * n)
                    split(b0 + 5 + 2 * n)

                def qk_copy(j, c):
                    if c < 3:
                        act.wait_ge(qk_ps, 3 * (4 * a + j) + c + 1)
                    else:
                        act.wait_ge(block_used, b0 + 4 + 2 * j + 2)
                    dst = (q_t if c < 2 else k_t)[:, j % 2, c % 2, :]
                    act.activation(dst, bank[c][:, 0:SEQ], ACT.Copy,
                                   scale=HEAD_DIM ** -0.5 if c < 2 else 1.0).then_inc(qk_done, 1)

                def attend(h):
                    act.wait_ge(log_att_done, HEADS * a + h + 1)
                    act.activation(att[:, h % 2, :], log_att[:, h % 2, :], ACT.Exp).then_inc(att_done, 1)

                def o_copy(j):
                    act.wait_ge(o_ps, 4 * a + j + 1)
                    act.activation(o_sb[:, :, :], tb[1][:, :].rearrange("p (h c) -> p h c", h=2),
                                   ACT.Copy).then_inc(o_done, 1)

                def o_hi(j):
                    act.wait_ge(mt_ps, mtp_base(p) + j + 1)
                    act.activation(mt_hi[:, 2 * j:2 * j + 2, :], tb[0][:, :].rearrange("p (j t) -> p j t", j=2),
                                   ACT.Copy).then_inc(mt_hi_done, 1)

                for c in range(4):
                    qk_copy(0, c)
                for j in range(4):
                    split(b0 + 8 + 2 * j)
                    for m in range(HEADS_PER_J):
                        h = HEADS_PER_J * j + m
                        H = HEADS * a + h
                        act.wait_ge(z_ps, H + 1)
                        act.activation(z_abs[:, h % 2, :], up[h % 2][:, 0:384], ACT.Abs).then_inc(abs_done, 1)
                        if h >= 1:
                            attend(h - 1)
                        act.wait_ge(abs_done, H + 1)
                        act.activation(z_exp[:, h % 2, :], z_abs[:, h % 2, :], ACT.Exp, scale=-1.0).then_inc(exp_done, 1)
                        act.wait_ge(exp_done, H + 1)
                        act.activation(z_ln[:, h % 2, :], z_exp[:, h % 2, :], ACT.Ln, bias=1.0).then_inc(ln_done, 1)
                        if j >= 1 and m == 0:
                            o_copy(j - 1)
                        if j >= 1 and m == 1:
                            o_hi(j - 1)
                        if j < 3 and m == 2:
                            split(b0 + 9 + 2 * j)
                        if j < 3 and m >= 2:
                            qk_copy(j + 1, 2 * m - 4)
                            qk_copy(j + 1, 2 * m - 3)
                attend(HEADS - 1)
                o_copy(3)
                o_hi(3)
                for i in (15, 16, 17):
                    split(b0 + i)

            def ssd(p):
                b0 = base[p]
                split(b0 + 2)
                act.add_instruction(mybir.InstLoadActFuncSet(
                    act_func_set_id=LOG_EXP_SET, name=nc.get_next_instruction_name(),
                    engine=mybir.EngineType.Activation))
                def small_vectors():
                    act.wait_ge(cum2_ps, 1)
                    act.activation(acum[:, :], tb[1][:, 0:CH], ACT.Copy).then_inc(dt_act, 1)
                    act.wait_ge(dt_act, 5)
                    act.activation(e_off[:, :], acum[:, SSD_HEADS:CH], ACT.Exp).then_inc(dt_act, 1)
                    act.wait_ge(dt_dve, 10)
                    act.activation(to_end[:, :], dts[:, 7, 0:SSD_HEADS], ACT.Exp).then_inc(dt_act, 1)

                act.wait_ge(dt_dve, 1)
                act.activation(dts[:, 1, :], dts[:, 0, :], ACT.Abs).then_inc(dt_act, 1)
                act.wait_ge(dt_act, 1)
                act.activation(dts[:, 2, :], dts[:, 1, :], ACT.Exp, scale=-1.0).then_inc(dt_act, 1)
                act.wait_ge(dt_act, 2)
                act.activation(dts[:, 3, :], dts[:, 2, :], ACT.Ln, bias=1.0).then_inc(dt_act, 1)
                act.wait_ge(bc_in, 48)
                act.activation(dts[:, 8, 0:SSD_HEADS], a_log_bc[:, :], ACT.Exp).then_inc(dt_act, 1)
                split(b0 + 3)

                def z_copy(n):
                    for h in range(HALVES):
                        if h == 0:
                            act.wait_ge(zz_ps, n + 1)
                        else:
                            act.wait_ge(block_used, b0 + 2 * n + 3)
                        act.activation(z_sb[:, h, 512 * n:512 * (n + 1)], up[h][:, :], ACT.Copy).then_inc(zz_done, 1)

                def decay_exp(s):
                    act.wait_ge(seg_done, SSD_HPG * (s + 1))
                    d = decay[:, s // 2, s % 2, :, :]
                    act.activation(d, d, ACT.Exp).then_inc(decay_done, 1)

                for n in range(4):
                    split(b0 + 4 + 2 * n)
                    z_copy(n)
                    if n == 0:
                        small_vectors()
                    split(b0 + 5 + 2 * n)
                    for s in range(4 * n, 4 * n + 4):
                        decay_exp(s)

                def conv_first(g, c):
                    k = ssd_chunk(g, c)
                    if c < 3:
                        act.wait_ge(raw_ps, raw_base(p) + 3 * g + c + 1)
                    else:
                        act.wait_ge(block_used, b0 + 11 + 2 * g)
                    if g >= 1:
                        act.wait_ge(chan_done, chan_base(p) + 4 * (g - 1) + c + 1)
                    t = TAPS + (SSD_CONV - 1) * (SSD_CONV_DIM // P) + k
                    act.activation(chan[:, c, :], bank[c][:, 0:SEQ], ACT.Identity,
                                   bias=par[:, CBIAS + k:CBIAS + k + 1], scale=par[:, t:t + 1]).then_inc(tap_first, 1)

                def conv_silu(g, c):
                    act.wait_ge(tap_done, tap_base(p) + 3 * (4 * g + c + 1))
                    act.activation(chan[:, c, :], chan[:, c, :], ACT.Silu).then_inc(chan_done, 1)

                def conv_group(g):
                    for c in range(4):
                        conv_first(g, c)
                        if c >= 1:
                            conv_silu(g, c - 1)
                    conv_silu(g, 3)

                def y_hi(g):
                    act.wait_ge(mt_src, src_base(p) + g + 1)
                    act.activation(mt_hi[:, 2 * g:2 * g + 2, :], yg[:, :, :], ACT.Copy).then_inc(mt_hi_done, 1)

                split(b0 + 12)
                conv_group(0)
                for g in range(SSD_G):
                    split(b0 + 13 + 2 * g)
                    if g >= 1:
                        y_hi(g - 1)
                    act.wait_ge(tok_ps, 2 * g + 2)
                    act.activation(b_tok, tb[1][:, 256:384], ACT.Copy).then_inc(tok_act, 1)
                    z = z_sb[:, :, 256 * g:256 * (g + 1)]
                    if g == 0:
                        act.wait_ge(zz_done, 8)
                    act.activation(z, z, ACT.Silu).then_inc(y_act, 1)
                    act.wait_ge(hp_ps, g + 1)
                    act.activation(h_prev, up[1][:, 0:256], ACT.Copy).then_inc(hp_done, 1)
                    if g < SSD_G - 1:
                        split(b0 + 14 + 2 * g)
                        conv_group(g + 1)
                    act.wait_ge(y_step, 5 * (g + 1))
                    for h in range(HALVES):
                        act.activation(xd[:, h, :], y_sb[:, h, :], ACT.Square,
                                       accum_out=yss[:, h:h + 1]).then_inc(y_act, 1)
                y_hi(SSD_G - 1)
                for i in range(28, 35):
                    split(b0 + i)

            def conv_mixer(p):
                b0 = base[p]
                split(b0 + 2)
                for j in range(KD):
                    b = j % 2
                    split(b0 + 3 + 2 * j)
                    act.wait_ge(raw_ps, raw_base(p) + 2 * j + 1)
                    act.activation(c_sb[:, b, :], bank[3 * b][:, 0:SEQ], ACT.Copy).then_inc(chan_done, 1)
                    act.wait_ge(tap_done, tap_base(p) + 3 * j + 1)
                    t = SCTAPS + (SC_W - 1) * KD + j
                    act.activation(u_sb[:, b, :], ch[:, b, :], ACT.Copy, scale=par[:, t:t + 1]).then_inc(tap_first, 1)
                    act.wait_ge(mt_src, src_base(p) + j + 1)
                    act.activation(mt_hi[:, j, :], bu[:, b, :], ACT.Copy).then_inc(mt_hi_done, 1)
                    if j < KD - 1:
                        split(b0 + 4 + 2 * j)
                split(b0 + 18)
                for i in range(19, 22):
                    split(b0 + i)

            split(0)
            split(1)
            act.wait_ge(par_ps, 1)
            act.activation(par[:, :], tb[0][:, 0:N_NORM + N_TAP + N_REST], ACT.Copy).then_inc(par_sb, 1)
            for p, (kind, _, _) in enumerate(PHASES):
                entry(p)
                {"ffn": ffn, "attention": attention, "ssd": ssd, "conv": conv_mixer}[kind](p)
            entry(n_phases)

        @block.vector
        def _(dve):
            def split(n, step=None):
                if n >= total:
                    return
                s, q, c = n % STAGE_SLOTS, n % SPLIT_SLOTS, block_columns(n)
                dve.wait_ge(hi_done, at(n + 1, step, LOOP_BLOCKS))
                dve.tensor_tensor(w_lo[q][:, 0:c], stage[s][:, 0:c], w_hi[q][:, 0:c].bitcast(F32),
                                  ALU.subtract).then_inc(lo_done, 1)

            def by_column(columns, rest):
                return columns.unsqueeze(2).to_broadcast([P, columns.shape[1], rest])

            def update(p, i):
                kind = PHASES[p][0]
                h, n = i % 2, i // 2
                acc_wait(dve, p, i)
                xq = x_res[:, h, 512 * n:512 * (n + 1)]
                dve.scalar_tensor_tensor(xq, acc(i)[:, :], 0.5 if kind == "ffn" else 1.0, xq,
                                         ALU.mult, ALU.add).then_inc(x_updated, 1)

            def entry(p):
                kind = PHASES[p][0] if p < n_phases else None

                def upd(i):
                    if p >= 1:
                        update(p - 1, i)

                def gain(i):
                    n = i // 2
                    dve.wait_ge(xt_ps, QUARTERS * p + i + 1)
                    dve.tensor_tensor(xg[:, i, :].rearrange("p (k t) -> p k t", k=4),
                                      tb[i % 2][:, :].rearrange("p (k t) -> p k t", k=4),
                                      by_column(par[:, gains(p) + 4 * n:gains(p) + 4 * (n + 1)], P),
                                      ALU.mult).then_inc(xg_done, 1)

                def lo(i):
                    h, n = i % 2, i // 2
                    dve.wait_ge(xt_hi_done, QUARTERS * p + i + 1)
                    t = (slice(None), slice(4 * n, 4 * (n + 1)), slice(h * P, (h + 1) * P))
                    dve.tensor_tensor(xt_lo[t], xg[:, i, :].rearrange("p (k t) -> p k t", k=4),
                                      xt_hi[t].bitcast(F32), ALU.subtract).then_inc(xt_lo_done, 1)

                if kind == "ffn":
                    upd(0)
                    upd(1)
                    gain(0)
                    upd(2)
                    lo(0)
                    gain(1)
                    upd(3)
                    lo(1)
                    gain(2)
                    gain(3)
                    lo(2)
                    lo(3)
                    return
                for i in range(QUARTERS):
                    upd(i)
                dve.wait_ge(rstd_done, p + 1)
                for h in range(HALVES):
                    if kind is None:
                        dve.wait_ge(gain_in, 16)
                        dve.scalar_tensor_tensor(xn[:, h, :], x_res[:, h, :], rstd[:, h:h + 1], final_gain,
                                                 ALU.mult, ALU.mult).then_inc(xn_done, 1)
                    else:
                        dve.tensor_scalar(xn[:, h, :], x_res[:, h, :], rstd[:, h:h + 1], None,
                                          ALU.mult).then_inc(xn_done, 1)
                if kind is not None:
                    gain(0)
                    gain(1)
                    lo(0)
                    gain(2)
                    lo(1)
                    gain(3)
                    lo(2)
                    lo(3)

            def ffn(p):
                f = nth("ffn", p)

                def hidden_lo(g, step=None):
                    G = GROUPS * f + g
                    dve.wait_ge(ht_hi_done, at(G + 1, step, 2))
                    dve.tensor_tensor(ht_lo[:, :, :], tb[0][:, :].rearrange("p (j t) -> p j t", j=2),
                                      ht_hi[:, :, :].bitcast(F32), ALU.subtract).then_inc(ht_lo_done, 1)

                def gate(g, step=None):
                    G = GROUPS * f + g
                    for h in range(HALVES):
                        dve.wait_ge(silu_done, at(2 * G + h + 1, step, 4))
                        dve.scalar_tensor_tensor(hid[:, h, :], up[h][:, FFN_W:2 * FFN_W], rstd[:, h:h + 1],
                                                 sg[:, h, :], ALU.mult, ALU.mult).then_inc(gated, 1)

                def group(g, step=None):
                    if g >= 1:
                        split(base[p] + 3 * g + 1, step)
                        hidden_lo(g - 1, step)
                    split(base[p] + 3 * g + 2, step)
                    gate(g, step)
                    split(base[p] + 3 * g + 3, step)

                for g in range(LOOP_FROM):
                    group(g)
                with dve.Fori(0, (LOOP_TO - LOOP_FROM) // 2) as step:
                    for g in (LOOP_FROM, LOOP_FROM + 1):
                        group(g, step)
                group(GROUPS - 1)
                hidden_lo(GROUPS - 1)
                split(base[p + 1] + 1)

            def attention(p):
                a, b0 = nth("attention", p), base[p]
                for i in range(2, 8):
                    split(b0 + i)

                def weigh(h):
                    dve.wait_ge(cum_ps, HEADS * a + h + 1)
                    e = log_att[:, h % 2, :].rearrange("p (b c) -> p b c", b=3)
                    z = up[h % 2][:, 0:384].rearrange("p (b c) -> p b c", b=3)
                    dve.scalar_tensor_tensor(e[:, 0:3:2, :], z[:, 0:3:2, :], 0.0,
                                             bar[:, :].unsqueeze(1).to_broadcast([P, 2, P]), ALU.min, ALU.add)\
                       .then_inc(sp_step, 1)
                    dve.tensor_scalar(e[:, 1, :], z[:, 1, :], 0.0, None, ALU.min).then_inc(log_att_done, 1)

                def o_lo(j):
                    dve.wait_ge(mt_hi_done, mt_base(p) + j + 1)
                    dve.tensor_tensor(mt_lo[:, 2 * j:2 * j + 2, :], tb[0][:, :].rearrange("p (j t) -> p j t", j=2),
                                      mt_hi[:, 2 * j:2 * j + 2, :].bitcast(F32), ALU.subtract).then_inc(mt_lo_done, 1)

                for j in range(4):
                    split(b0 + 8 + 2 * j)
                    for m in range(HEADS_PER_J):
                        h = HEADS_PER_J * j + m
                        H = HEADS * a + h
                        if h >= 1:
                            weigh(h - 1)
                        dve.wait_ge(ln_done, H + 1)
                        dve.scalar_tensor_tensor(softplus[:, h % 2, :], up[h % 2][:, 0:384], 0.0,
                                                 z_ln[:, h % 2, :], ALU.max, ALU.add).then_inc(sp_step, 1)
                        dve.wait_ge(sp_step, HEADS * 2 * a + 2 * h + 1)
                        diag = softplus[:, h % 2, :].rearrange("p (b c) -> p b c", b=3)[:, 0:3:2, :]
                        dve.tensor_tensor(diag, diag, keep[:, :].unsqueeze(1).to_broadcast([P, 2, P]),
                                          ALU.mult).then_inc(sp_done, 1)
                        if j >= 1 and m == 1:
                            o_lo(j - 1)
                        if j < 3 and m == 2:
                            split(b0 + 9 + 2 * j)
                weigh(HEADS - 1)
                o_lo(3)
                for i in (15, 16, 17):
                    split(b0 + i)

            def chain(semaphore, value, instruction):
                instruction.then_inc(semaphore, 1)
                dve.wait_ge(semaphore, value)

            def ssd(p):
                b0 = base[p]
                split(b0 + 2)
                row = lambda k: dts[:, k, :]
                both = lambda v: v.unsqueeze(1).to_broadcast([P, 2, SSD_HEADS])
                pair = lambda v: v.rearrange("p (c h) -> p c h", c=2)
                dve.wait_ge(block_used, b0 + 1)
                dve.wait_ge(bc_in, 48)
                dve.tensor_tensor(pair(row(0)), pair(tb[0][:, 0:CH]), both(dt_bias_bc[:, :]), ALU.add).then_inc(dt_dve, 1)
                dve.wait_ge(dt_act, 3)
                chain(dt_dve, 2, dve.tensor_scalar(row(4), row(2), 1.0, None, ALU.add))
                chain(dt_dve, 3, dve.tensor_scalar(row(5), row(4), 1.0, None, ALU.subtract))
                chain(dt_dve, 4, dve.tensor_tensor(row(1), row(2), row(5), ALU.subtract))
                chain(dt_dve, 5, dve.reciprocal(row(2), row(4)))
                chain(dt_dve, 6, dve.tensor_tensor(row(5), row(1), row(2), ALU.mult))
                chain(dt_dve, 7, dve.scalar_tensor_tensor(row(4), row(0), 0.0, row(3), ALU.max, ALU.add))
                chain(dt_dve, 8, dve.tensor_tensor(row(6), row(4), row(5), ALU.add))
                dve.wait_ge(dt_act, 4)
                dve.scalar_tensor_tensor(pair(row(0)), pair(row(6)), -1.0, both(dts[:, 8, 0:SSD_HEADS]),
                                         ALU.mult, ALU.mult).then_inc(dt_dve, 1)
                split(b0 + 3)

                def segments(s):
                    g, c = divmod(s, 2)
                    dve.wait_ge(seg_ps, s + 1)
                    for r in range(SSD_HPG):
                        col = SSD_HEADS * c + SSD_HPG * g + r
                        dve.tensor_scalar(decay[:, g, c, r, :], tb[s % 2][:, r * P:(r + 1) * P],
                                          acum[:, col:col + 1], 0.0, ALU.subtract, ALU.min).then_inc(seg_done, 1)

                for n in range(4):
                    split(b0 + 4 + 2 * n)
                    if n == 0:
                        dve.wait_ge(dt_act, 5)
                        dve.tensor_tensor(dts[:, 7, 0:SSD_HEADS], tb[1][:, CH:CH + SSD_HEADS],
                                          acum[:, 0:SSD_HEADS], ALU.subtract).then_inc(dt_dve, 1)
                    split(b0 + 5 + 2 * n)
                    for s in range(4 * n, 4 * n + 4):
                        segments(s)

                def taps(g, c):
                    k = ssd_chunk(g, c)
                    dve.wait_ge(tap_first, chan_base(p) + 4 * g + c + 1)
                    for i in range(1, SSD_CONV):
                        t = TAPS + (SSD_CONV - 1 - i) * (SSD_CONV_DIM // P) + k
                        dve.scalar_tensor_tensor(chan[:, c, i:SEQ], bank[c][:, 0:SEQ - i], par[:, t:t + 1],
                                                 chan[:, c, i:SEQ], ALU.mult, ALU.add).then_inc(tap_done, 1)
                        dve.wait_ge(tap_done, tap_base(p) + 3 * (4 * g + c) + i)

                def y_gain(g):
                    dve.wait_ge(mt_ps, mtp_base(p) + g + 1)
                    dve.tensor_tensor(yg[:, :, :], tb[0][:, :].rearrange("p (c t) -> p c t", c=2),
                                      by_column(par[:, YNORM + 2 * g:YNORM + 2 * g + 2], SEQ),
                                      ALU.mult).then_inc(mt_src, 1)

                def y_lo(g):
                    dve.wait_ge(mt_hi_done, mt_base(p) + g + 1)
                    dve.tensor_tensor(mt_lo[:, 2 * g:2 * g + 2, :], yg[:, :, :],
                                      mt_hi[:, 2 * g:2 * g + 2, :].bitcast(F32), ALU.subtract).then_inc(mt_lo_done, 1)

                def heads(v):
                    return v.rearrange("p (r d) -> p r d", r=SSD_HPG)

                for c in range(4):
                    taps(0, c)
                for g in range(SSD_G):
                    split(b0 + 12) if g == 0 else None
                    split(b0 + 13 + 2 * g)
                    if g >= 1:
                        y_gain(g - 1)
                    h0 = SSD_HPG * g
                    dve.wait_ge(tok_ps, 2 * g + 1)
                    for h in range(HALVES):
                        x_tok = heads(tb[0][:, 256 * h:256 * (h + 1)])
                        col = SSD_HEADS * h + h0
                        last = dve.tensor_tensor(heads(xdt[:, h, :]), x_tok,
                                                 by_column(dts[:, 6, col:col + SSD_HPG], SSD_P), ALU.mult)
                        last.then_inc(xdt_done, 1)
                    dve.wait_ge(xdt_done, 2 * g + 1)
                    dve.wait_ge(dt_act, 7)
                    dve.tensor_tensor(heads(x_end), heads(xdt[:, 0, :]),
                                      by_column(to_end[:, h0:h0 + SSD_HPG], SSD_P), ALU.mult).then_inc(tok_dve, 1)
                    dve.wait_ge(tok_act, g + 1)
                    dve.tensor_tensor(cb[:, :, :], tb[1][:, 0:256].rearrange("p (c l) -> p c l", c=2),
                                      upper[:, :].unsqueeze(1).to_broadcast([P, 2, P]), ALU.mult).then_inc(tok_dve, 1)
                    for h in range(HALVES):
                        dve.tensor_tensor(heads(xd[:, h, :]), heads(tb[0][:, 256 * h:256 * (h + 1)]),
                                          by_column(d_bc[:, h0:h0 + SSD_HPG], SSD_P), ALU.mult).then_inc(tok_dve, 1)
                    if g >= 1:
                        y_lo(g - 1)
                    if g < SSD_G - 1:
                        split(b0 + 14 + 2 * g)
                        for c in range(3):
                            taps(g + 1, c)
                    dve.wait_ge(y_ps, g + 1)
                    dve.wait_ge(tok_dve, 4 * (g + 1))
                    dve.tensor_tensor(y_sb[:, 0, :], up[0][:, 0:256], xd[:, 0, :], ALU.add).then_inc(y_step, 1)
                    dve.tensor_tensor(heads(y_sb[:, 1, :]), heads(up[1][:, 256:512]),
                                      by_column(e_off[:, h0:h0 + SSD_HPG], SSD_P), ALU.mult).then_inc(y_step, 1)
                    chain(y_step, 5 * g + 3, dve.tensor_tensor(xd[:, 1, :], up[0][:, 256:512], xd[:, 1, :], ALU.add))
                    chain(y_step, 5 * g + 4, dve.tensor_tensor(y_sb[:, 1, :], y_sb[:, 1, :], xd[:, 1, :], ALU.add))
                    dve.wait_ge(y_act, 3 * g + 1)
                    dve.tensor_tensor(y_sb[:, :, :], y_sb[:, :, :], z_sb[:, :, 256 * g:256 * (g + 1)],
                                      ALU.mult).then_inc(y_step, 1)
                    if g < SSD_G - 1:
                        taps(g + 1, 3)
                    dve.wait_ge(y_rstd, g + 1)
                    for h in range(HALVES):
                        dve.tensor_scalar(y_sb[:, h, :], y_sb[:, h, :], yrstd[:, h:h + 1], None,
                                          ALU.mult).then_inc(y_done, 1)
                y_gain(SSD_G - 1)
                y_lo(SSD_G - 1)
                for i in range(28, 35):
                    split(b0 + i)

            def conv_mixer(p):
                b0 = base[p]
                split(b0 + 2)
                for j in range(KD):
                    b = j % 2
                    split(b0 + 3 + 2 * j)
                    dve.wait_ge(raw_ps, raw_base(p) + 2 * j + 2)
                    dve.wait_ge(chan_done, chan_base(p) + j + 1)
                    dve.tensor_tensor(ch[:, b, :], bank[3 * b + 1][:, 0:SEQ], c_sb[:, b, :], ALU.mult).then_inc(tap_done, 1)
                    dve.wait_ge(tap_first, chan_base(p) + j + 1)
                    for i in range(1, SC_W):
                        t = SCTAPS + (SC_W - 1 - i) * KD + j
                        dve.scalar_tensor_tensor(u_sb[:, b, i:SEQ], ch[:, b, 0:SEQ - i], par[:, t:t + 1],
                                                 u_sb[:, b, i:SEQ], ALU.mult, ALU.add).then_inc(tap_done, 1)
                        dve.wait_ge(tap_done, tap_base(p) + 3 * j + i + 1)
                    dve.wait_ge(block_used, b0 + 2 * j + 2)
                    dve.tensor_tensor(bu[:, b, :], bank[3 * b + 2][:, 0:SEQ], u_sb[:, b, :], ALU.mult).then_inc(mt_src, 1)
                    dve.wait_ge(mt_hi_done, mt_base(p) + j + 1)
                    dve.tensor_tensor(mt_lo[:, j, :], bu[:, b, :], mt_hi[:, j, :].bitcast(F32),
                                      ALU.subtract).then_inc(mt_lo_done, 1)
                    if j < KD - 1:
                        split(b0 + 4 + 2 * j)
                for i in range(18, 22):
                    split(b0 + i)

            split(0)
            split(1)
            dve.wait_ge(par_sb, 1)
            dve.wait_ge(const_done, 5)
            for p, (kind, _, _) in enumerate(PHASES):
                entry(p)
                {"ffn": ffn, "attention": attention, "ssd": ssd, "conv": conv_mixer}[kind](p)
            entry(n_phases)

        @block.tensor
        def _(pe):
            def products(out_, stationary, moving, start, stop):
                pe.matmul(out_, stationary[0], moving[0], start=start, stop=False)
                pe.matmul(out_, stationary[0], moving[1], start=False, stop=False)
                return pe.matmul(out_, stationary[1], moving[0], start=False, stop=stop)

            def block_in(n, step=None):
                pe.wait_ge(lo_done, at(n + 1, step, LOOP_BLOCKS))

            def w_pair(n, c0, cols):
                q = n % SPLIT_SLOTS
                return w_hi[q][:, c0:c0 + cols], w_lo[q][:, c0:c0 + cols]

            def x_pair(k, t0=0, tokens=SEQ):
                return xt_hi[:, k, t0:t0 + tokens], xt_lo[:, k, t0:t0 + tokens]

            def transpose_entry(p, i):
                if p >= n_phases:
                    return
                h, n = i % 2, i // 2
                if PHASES[p][0] == "ffn":
                    src = x_res
                    if p == 0:
                        pe.wait_ge(x_in, 16 * HALVES)
                    else:
                        pe.wait_ge(x_updated, QUARTERS * (p - 1) + i + 1)
                else:
                    src = xn
                    pe.wait_ge(xn_done, 2 * mixers_before(p) + h + 1)
                if i >= 2:
                    pe.wait_ge(xg_done, QUARTERS * p + i - 1)
                for k in range(4):
                    mm = pe.transpose(tb[i % 2][:, k * P:(k + 1) * P],
                                      src[:, h, 512 * n + k * P:512 * n + (k + 1) * P], ident[:, :])
                mm.then_inc(xt_ps, 1)

            def entry_early(p, i):
                if p < n_phases and PHASES[p][0] == "ffn" and i >= 2:
                    transpose_entry(p, i - 2)

            def entry_rest(p):
                early = 2 if p < n_phases and PHASES[p][0] == "ffn" and p > 0 else 0
                for i in range(early, QUARTERS):
                    transpose_entry(p, i)

            def ffn(p):
                f = nth("ffn", p)

                def gate_up(g, kh, step=None):
                    G = GROUPS * f + g
                    n = (blk_a, blk_b)[kh](p, g)
                    block_in(n, step)
                    for h in range(HALVES):
                        if g == 0:
                            pe.wait_ge(xt_lo_done, QUARTERS * p + 2 * kh + h + 1)
                        if kh == 0 and G >= 1:
                            pe.wait_ge(gated, at(2 * (G - 1) + h + 1, step, 4))
                        for k in range(4):
                            mm = products(up[h][:, :], x_pair(4 * kh + k, h * P, P), w_pair(n, 512 * k, 512),
                                          start=kh == 0 and k == 0, stop=kh == 1 and k == 3)
                        if kh == 1 and h == 0:
                            mm.then_inc(half0_done, 1)
                    mm.then_inc(block_used, 1)

                def hidden_t(g, step=None):
                    G = GROUPS * f + g
                    pe.wait_ge(gated, at(2 * G + 2, step, 4))
                    for j in range(2):
                        for h in range(HALVES):
                            mm = pe.transpose(tb[0][:, j * SEQ + h * P:j * SEQ + (h + 1) * P],
                                              hid[:, h, j * P:(j + 1) * P], ident[:, :])
                    mm.then_inc(ht_ps, 1)

                def down(g, step=None):
                    G = GROUPS * f + g
                    n = blk_d(p, g)
                    block_in(n, step)
                    pe.wait_ge(ht_lo_done, at(G + 1, step, 2))
                    for i in range(QUARTERS):
                        h, nb = i % 2, i // 2
                        for j in range(2):
                            t = (slice(None), j, slice(h * P, (h + 1) * P))
                            mm = products(acc(i)[:, :], (ht_hi[t], ht_lo[t]), w_pair(n, D * j + 512 * nb, 512),
                                          start=g == 0 and j == 0, stop=g == GROUPS - 1 and j == 1)
                        if g == GROUPS - 1 and i < 3:
                            mm.then_inc(acc_ready, 1)
                        if i == 3:
                            mm.then_inc(block_used, 1)
                        if g == GROUPS - 1:
                            entry_early(p + 1, i)

                def group(g, step=None):
                    gate_up(g, 0, step)
                    if g >= 1:
                        hidden_t(g - 1, step)
                    gate_up(g, 1, step)
                    if g >= 1:
                        down(g - 1, step)

                for g in range(LOOP_FROM):
                    group(g)
                with pe.Fori(0, (LOOP_TO - LOOP_FROM) // 2) as step:
                    for g in (LOOP_FROM, LOOP_FROM + 1):
                        group(g, step)
                group(GROUPS - 1)
                hidden_t(GROUPS - 1)
                down(GROUPS - 1)

            def out_projection(p):
                kind = PHASES[p][0]
                first, nk = out_blocks(kind)
                count = {"attention": 4, "ssd": SSD_G, "conv": KD}[kind]
                pe.wait_ge(mt_lo_done, mt_base(p) + count)
                for nb in range(NB):
                    for kq in range(nk):
                        n = base[p] + first + nk * nb + kq
                        block_in(n)
                        for h in range(HALVES):
                            i = 2 * nb + h
                            for k in range(4):
                                t = (slice(None), 4 * kq + k, slice(h * P, (h + 1) * P))
                                mm = products(acc(i)[:, :], (mt_hi[t], mt_lo[t]), w_pair(n, 512 * k, 512),
                                              start=kq == 0 and k == 0, stop=kq == nk - 1 and k == 3)
                            if h == 1:
                                mm.then_inc(block_used, 1)
                            elif kq == nk - 1:
                                mm.then_inc(acc_ready, 1)
                            if kq == nk - 1:
                                entry_early(p + 1, i)

            def by_channel(n, kh, c, width, out_, signal):
                for k in range(4):
                    mm = products(out_, w_pair(n, width * k + P * c, P), x_pair(4 * kh + k),
                                  start=kh == 0 and k == 0, stop=kh == 1 and k == 3)
                if signal is not None:
                    mm.then_inc(signal, 1)

            def attention(p):
                a, b0 = nth("attention", p), base[p]
                pe.wait_ge(xt_lo_done, QUARTERS * (p + 1))
                for nb in range(NB):
                    for kh in range(2):
                        n = b0 + 2 * nb + kh
                        block_in(n)
                        for h in range(HALVES):
                            for k in range(4):
                                mm = products(bank[4 + 2 * nb + h][:, :], x_pair(4 * kh + k, h * P, P),
                                              w_pair(n, 512 * k, 512),
                                              start=kh == 0 and k == 0, stop=kh == 1 and k == 3)
                            if kh == 1 and h == 0:
                                mm.then_inc(v_ps, 1)
                        mm.then_inc(block_used, 1)

                def qk_slice(j, s):
                    kh, c = divmod(s, 4)
                    n = b0 + 4 + 2 * j + kh
                    if c == 0:
                        block_in(n)
                    if kh == 0 and j >= 1:
                        pe.wait_ge(qk_done, 4 * (4 * a + j - 1) + c + 1)
                    by_channel(n, kh, c, 512, bank[c][:, 0:SEQ],
                               block_used if c == 3 else (qk_ps if kh == 1 else None))

                def scores(h):
                    j, m = divmod(h, HEADS_PER_J)
                    H = HEADS * a + h
                    pe.wait_ge(qk_done, 4 * (4 * a + j + 1))
                    if h >= 2:
                        pe.wait_ge(log_att_done, H - 1)
                    elif h == 0:
                        pe.wait_ge(v_done, 4 * a + 2)
                    r = HEAD_DIM * (m % 2)
                    kk, qq = k_t[r:r + HEAD_DIM, j % 2, m // 2, :], q_t[r:r + HEAD_DIM, j % 2, m // 2, :]
                    z = up[h % 2]
                    pe.matmul(z[:, 0:SEQ], kk[:, 0:P], qq, start=True, stop=True, skip_group_check=True)
                    pe.matmul(z[:, SEQ:SEQ + P], kk[:, P:SEQ], qq[:, P:SEQ], start=False, stop=True,
                              skip_group_check=True).then_inc(z_ps, 1)

                def cumulate(h):
                    pe.wait_ge(sp_done, HEADS * a + h + 1)
                    z, s = up[h % 2], softplus[:, h % 2, :]
                    pe.matmul(z[:, 0:SEQ], neg_lower[:, :], s[:, 0:SEQ], start=False, stop=True, skip_group_check=True)
                    pe.matmul(z[:, P:SEQ], neg_ones[:, :], s[:, SEQ:SEQ + P], start=False, stop=True,
                              skip_group_check=True)
                    pe.matmul(z[:, SEQ:SEQ + P], neg_lower[:, :], s[:, SEQ:SEQ + P], start=False, stop=True,
                              skip_group_check=True).then_inc(cum_ps, 1)

                def values(h):
                    j, m = divmod(h, HEADS_PER_J)
                    pe.wait_ge(att_done, HEADS * a + h + 1)
                    if m == 0:
                        if j == 0:
                            pe.wait_ge(v_done, 4 * (a + 1))
                        else:
                            pe.wait_ge(o_done, 4 * a + j)
                    w = att[:, h % 2, :]
                    v = lambda kb: v_sb[:, kb, h * HEAD_DIM:(h + 1) * HEAD_DIM]
                    o = lambda qb: tb[1][:, 256 * qb + HEAD_DIM * m:256 * qb + HEAD_DIM * (m + 1)]
                    pe.matmul(o(0), w[:, 0:P], v(0), start=True, stop=True)
                    pe.matmul(o(1), w[:, P:SEQ], v(0), start=True, stop=False)
                    mm = pe.matmul(o(1), w[:, SEQ:SEQ + P], v(1), start=False, stop=True)
                    if m == HEADS_PER_J - 1:
                        mm.then_inc(o_ps, 1)

                def o_transpose(j):
                    pe.wait_ge(o_done, 4 * a + j + 1)
                    if j >= 1:
                        pe.wait_ge(mt_lo_done, mt_base(p) + j)
                    for c in range(2):
                        for h in range(HALVES):
                            mm = pe.transpose(tb[0][:, c * SEQ + h * P:c * SEQ + (h + 1) * P],
                                              o_sb[:, h, c * P:(c + 1) * P], ident[:, :])
                    mm.then_inc(mt_ps, 1)

                for s in range(8):
                    qk_slice(0, s)
                for j in range(4):
                    for m in range(HEADS_PER_J):
                        h = HEADS_PER_J * j + m
                        if j < 3:
                            qk_slice(j + 1, 2 * m)
                        scores(h)
                        if h >= 1:
                            cumulate(h - 1)
                        if j >= 1 and m == 1:
                            o_transpose(j - 1)
                        if j < 3:
                            qk_slice(j + 1, 2 * m + 1)
                        if h >= 1:
                            values(h - 1)
                cumulate(HEADS - 1)
                values(HEADS - 1)
                o_transpose(3)
                out_projection(p)

            def ssd(p):
                b0 = base[p]
                pe.wait_ge(xt_lo_done, QUARTERS * (p + 1))
                block_in(b0)
                for h in range(HALVES):
                    for k in range(KD):
                        mm = products(tb[0][:, SSD_HEADS * h:SSD_HEADS * (h + 1)], x_pair(k, h * P, P),
                                      w_pair(b0, SSD_HEADS * k, SSD_HEADS), start=k == 0, stop=k == KD - 1)
                mm.then_inc(block_used, 1)

                def z_block(nb):
                    for kh in range(2):
                        n = b0 + 1 + 2 * nb + kh
                        block_in(n)
                        for h in range(HALVES):
                            if kh == 0 and nb >= 1:
                                pe.wait_ge(zz_done, 2 * (nb - 1) + h + 1)
                            for k in range(4):
                                mm = products(up[h][:, :], x_pair(4 * kh + k, h * P, P), w_pair(n, 512 * k, 512),
                                              start=kh == 0 and k == 0, stop=kh == 1 and k == 3)
                            if kh == 1 and h == 0:
                                mm.then_inc(zz_ps, 1)
                        mm.then_inc(block_used, 1)

                for nb in range(4):
                    z_block(nb)
                    if nb == 0:
                        pe.wait_ge(dt_dve, 9)
                        for c in range(2):
                            pe.matmul(tb[1][:, SSD_HEADS * c:SSD_HEADS * (c + 1)], upper[:, :],
                                      dts[:, 0, SSD_HEADS * c:SSD_HEADS * (c + 1)], start=True, stop=True)
                        pe.matmul(tb[1][:, CH:CH + SSD_HEADS], ones[:, :], dts[:, 0, 0:SSD_HEADS],
                                  start=True, stop=True).then_inc(cum2_ps, 1)
                    for s in range(4 * nb, 4 * nb + 4):
                        g, c = divmod(s, 2)
                        if s >= 2:
                            pe.wait_ge(seg_done, SSD_HPG * (s - 1))
                        elif s == 1:
                            pe.wait_ge(dt_dve, 10)
                        for r in range(SSD_HPG):
                            col = SSD_HEADS * c + SSD_HPG * g + r
                            mm = pe.matmul(tb[s % 2][:, r * P:(r + 1) * P],
                                           dts[:, 0, col:col + 1].to_broadcast([P, P]), upper[:, :],
                                           start=True, stop=True)
                        mm.then_inc(seg_ps, 1)

                def xbc_slice(g, s):
                    kh, c = divmod(s, 4)
                    n = b0 + 9 + 2 * g + kh
                    if c == 0:
                        block_in(n)
                    if kh == 0 and g >= 1:
                        pe.wait_ge(tap_done, tap_base(p) + 3 * (4 * (g - 1) + c + 1))
                    by_channel(n, kh, c, 512, bank[c][:, 0:SEQ],
                               block_used if c == 3 else (raw_ps if kh == 1 else None))

                def to_tokens(g):
                    pe.wait_ge(chan_done, chan_base(p) + 4 * (g + 1))
                    if g >= 1:
                        pe.wait_ge(mt_src, src_base(p) + g)
                    else:
                        pe.wait_ge(seg_done, SSD_HPG * 2 * SSD_G)
                    for h in range(HALVES):
                        for c in range(2):
                            mm = pe.transpose(tb[0][:, 256 * h + P * c:256 * h + P * (c + 1)],
                                              chan[:, c, h * P:(h + 1) * P], ident[:, :])
                    mm.then_inc(tok_ps, 1)
                    for c in range(2):
                        pe.matmul(tb[1][:, c * P:(c + 1) * P], chan[:, 2, c * P:(c + 1) * P],
                                  chan[:, 3, c * P:(c + 1) * P], start=True, stop=True)
                    pe.transpose(tb[1][:, 256:384], chan[:, 2, 0:P], ident[:, :]).then_inc(tok_ps, 1)

                def diagonal(g):
                    pe.wait_ge(tok_act, g + 1)
                    pe.wait_ge(tok_dve, 4 * g + 1)
                    if g >= 1:
                        pe.wait_ge(y_step, 5 * (g - 1) + 3)
                    else:
                        pe.wait_ge(zz_done, 8)
                    pe.matmul(up[1][:, 0:256], b_tok, x_end, start=True, stop=True).then_inc(hp_ps, 1)
                    pe.wait_ge(xdt_done, 2 * (g + 1))
                    for c in range(2):
                        pe.wait_ge(wdec_done, 2 * g + c + 1)
                        for r in range(SSD_HPG):
                            pe.matmul(up[0][:, 256 * c + SSD_P * r:256 * c + SSD_P * (r + 1)], decay[:, g, c, r, :],
                                      xdt[:, c, SSD_P * r:SSD_P * (r + 1)], start=True, stop=True)

                def carried(g):
                    pe.wait_ge(hp_done, g + 1)
                    pe.matmul(up[1][:, 256:512], chan[:, 3, P:SEQ], h_prev, start=True, stop=True).then_inc(y_ps, 1)

                def y_transpose(g):
                    pe.wait_ge(y_done, 2 * (g + 1))
                    for c in range(2):
                        for h in range(HALVES):
                            mm = pe.transpose(tb[0][:, c * SEQ + h * P:c * SEQ + (h + 1) * P],
                                              y_sb[:, h, c * P:(c + 1) * P], ident[:, :])
                    mm.then_inc(mt_ps, 1)

                for s in range(8):
                    xbc_slice(0, s)
                for g in range(SSD_G):
                    nxt = g + 1 < SSD_G
                    for s in range(2):
                        if nxt:
                            xbc_slice(g + 1, s)
                    if g >= 1:
                        y_transpose(g - 1)
                    if nxt:
                        xbc_slice(g + 1, 2)
                    to_tokens(g)
                    for s in (3, 4):
                        if nxt:
                            xbc_slice(g + 1, s)
                    diagonal(g)
                    for s in (5, 6):
                        if nxt:
                            xbc_slice(g + 1, s)
                    carried(g)
                    if nxt:
                        xbc_slice(g + 1, 7)
                y_transpose(SSD_G - 1)
                out_projection(p)

            def conv_mixer(p):
                b0 = base[p]
                pe.wait_ge(xt_lo_done, QUARTERS * (p + 1))
                for j in range(KD):
                    if j >= 2:
                        pe.wait_ge(mt_src, src_base(p) + j - 1)
                    for kh in range(2):
                        n = b0 + 2 * j + kh
                        block_in(n)
                        for c in range(3):
                            by_channel(n, kh, c, 3 * P, bank[3 * (j % 2) + c][:, 0:SEQ],
                                       block_used if c == 2 else (raw_ps if kh == 1 else None))
                out_projection(p)

            pe.wait_ge(const_done, 5)
            pe.wait_ge(par_in, 16 * 7)
            for t, n_rows, c0 in ((0, N_NORM, 0), (1, N_TAP, N_NORM), (2, N_REST, N_NORM + N_TAP)):
                mm = pe.transpose(tb[0][:, c0:c0 + n_rows], par_rows[0:n_rows, t, :], ident[0:n_rows, 0:n_rows])
            mm.then_inc(par_ps, 1)
            pe.wait_ge(par_sb, 1)
            for p, (kind, _, _) in enumerate(PHASES):
                entry_rest(p)
                {"ffn": ffn, "attention": attention, "ssd": ssd, "conv": conv_mixer}[kind](p)


_INS = ["x", "ffn1_norm", "ffn1_w_gu", "ffn1_w_down", "mix_norm", "ffn2_norm", "ffn2_w_gu", "ffn2_w_down",
        "sb_w_qkv", "sb_w_o", "ssd_w_in", "ssd_conv_w", "ssd_conv_b", "ssd_dt_bias", "ssd_a_log", "ssd_d",
        "ssd_norm", "ssd_w_out", "sc_w_in", "sc_conv_w", "sc_w_out", "final_norm"]


def kernel(**inputs):
    import numpy as np
    import concourse.bacc as bacc
    from concourse.bass_utils import run_bass_kernel_spmd

    nc = bacc.Bacc("TRN2", target_bir_lowering=False, num_devices=1)
    arrays, args = {}, []
    for name in _INS:
        a = np.ascontiguousarray(inputs[name])
        arrays[f"in_{name}"] = a
        args.append(nc.dram_tensor(f"in_{name}", a.shape, mybir.dt.from_np(a.dtype), kind="ExternalInput").ap())
    out = nc.dram_tensor("out", (1, SEQ, D), F32, kind="ExternalOutput").ap()
    build_trunk(nc, *args, out)
    r = run_bass_kernel_spmd(nc, [arrays], core_ids=[0])
    return r.results[0]["out"]
```
